# Optimizing a Trainium2 kernel written in Bass

```python
import jax, jax.numpy as jnp
from jax import lax
import numpy as np

D_MODEL = 1024
BATCH = 1
SEQ = 512
DEPTH = 4
DEC_BATCH = 1
DEC_SEQ = 64
PAST_LEN = 256

CHUNK = 64
N_MIXERS = 3
N_SB = (DEPTH + 2) // 3
N_CONV = (DEPTH + 1) // 3
N_GLA = DEPTH // 3
SB_HEADS = 16
SB_HEAD_DIM = D_MODEL // SB_HEADS
SB_Q_BLOCK = 128
CONV_WIDTH = 3
GLA_HEADS = 4
GLA_KEY_DIM = D_MODEL // 2
GLA_VALUE_DIM = D_MODEL
GLA_DK = GLA_KEY_DIM // GLA_HEADS
GLA_DV = GLA_VALUE_DIM // GLA_HEADS
GLA_GATE_RANK = 16
GLA_GATE_NORMALIZER = 16.0
GLA_IN_DIM = 2 * GLA_KEY_DIM + 2 * GLA_VALUE_DIM + GLA_GATE_RANK
MLP_HIDDEN = 4 * D_MODEL
NORM_EPS = 1e-6

kernel_name = 'hybrid_stickbreak_shortconv_gla_stream_step'

def rms_norm(x, gain):
    xf = x.astype(jnp.float32)
    y = xf * lax.rsqrt(jnp.mean(xf * xf, axis=-1, keepdims=True) + NORM_EPS)
    return (y * gain.astype(jnp.float32)).astype(x.dtype)

def sq_relu_mlp(x, w_up, w_down):
    h = jax.nn.relu(x @ w_up)
    return (h * h) @ w_down

def stick_breaking_block(q, k, v, q_pos, k_pos):
    z = jnp.einsum('bqhd,bkhd->bhqk', q.astype(jnp.float32), k.astype(jnp.float32)) * (SB_HEAD_DIM ** -0.5)
    mask = k_pos[None, :] < q_pos[:, None]
    log_not = jnp.where(mask, jax.nn.log_sigmoid(-z), 0.0)
    rev = lax.cumsum(log_not, axis=3, reverse=True)
    tail = jnp.pad(rev[..., 1:], ((0, 0), (0, 0), (0, 0), (0, 1)))
    a = jnp.where(mask, jnp.exp(jax.nn.log_sigmoid(z) + tail), 0.0)
    return jnp.einsum('bhqk,bkhd->bqhd', a, v.astype(jnp.float32))

def sb_project(h, w_qkv):
    b, t, _ = h.shape
    qkv = (h @ w_qkv).reshape(b, t, 3, SB_HEADS, SB_HEAD_DIM)
    return qkv[:, :, 0], qkv[:, :, 1], qkv[:, :, 2]

def sb_mix_prompt(h, w_qkv, w_o):
    b, t, _ = h.shape
    q, k, v = sb_project(h, w_qkv)
    nb = t // SB_Q_BLOCK
    q_blocks = q.reshape(b, nb, SB_Q_BLOCK, SB_HEADS, SB_HEAD_DIM).transpose(1, 0, 2, 3, 4)
    pos = jnp.arange(t, dtype=jnp.int32)
    pos_blocks = pos.reshape(nb, SB_Q_BLOCK)
    o = lax.map(lambda qp: stick_breaking_block(qp[0], k, v, qp[1], pos), (q_blocks, pos_blocks))
    o = o.transpose(1, 0, 2, 3, 4).reshape(b, t, D_MODEL).astype(h.dtype)
    return o @ w_o, k, v

def sb_mix_sample(h, cache_k, cache_v, w_qkv, w_o):
    b, t, _ = h.shape
    q, k, v = sb_project(h, w_qkv)
    past = cache_k.shape[1]
    k_all = jnp.concatenate([cache_k.astype(k.dtype), k], axis=1)
    v_all = jnp.concatenate([cache_v.astype(v.dtype), v], axis=1)
    q_pos = past + jnp.arange(t, dtype=jnp.int32)
    k_pos = jnp.arange(past + t, dtype=jnp.int32)
    o = stick_breaking_block(q, k_all, v_all, q_pos, k_pos).reshape(b, t, D_MODEL).astype(h.dtype)
    return o @ w_o, k, v

def short_conv_mix(h, conv_prefix, w_in, w_conv, w_out):
    gate_b, gate_c, xp = jnp.split(h @ w_in, 3, axis=-1)
    u = gate_c * xp
    u_ext = jnp.concatenate([conv_prefix.astype(u.dtype), u], axis=1)
    t = h.shape[1]
    y = w_conv[0] * u_ext[:, 0:t]
    for i in range(1, CONV_WIDTH):
        y = y + w_conv[i] * u_ext[:, i:i + t]
    return (gate_b * y) @ w_out, u_ext[:, -(CONV_WIDTH - 1):]

def gla_project(h, w_in, w_gk2, b_gk):
    b, t, _ = h.shape
    splits = [GLA_KEY_DIM, 2 * GLA_KEY_DIM, 2 * GLA_KEY_DIM + GLA_VALUE_DIM, 2 * GLA_KEY_DIM + 2 * GLA_VALUE_DIM]
    q, k, v, g_out, gk_low = jnp.split(h @ w_in, splits, axis=-1)
    gk = jax.nn.log_sigmoid((gk_low @ w_gk2 + b_gk).astype(jnp.float32)) / GLA_GATE_NORMALIZER

    def heads(a, dh):
        return a.reshape(b, t, GLA_HEADS, dh).transpose(0, 2, 1, 3).astype(jnp.float32)

    return heads(q, GLA_DK) * (GLA_DK ** -0.5), heads(k, GLA_DK), heads(v, GLA_DV), heads(gk, GLA_DK), g_out

def gla_chunk(state, q, k, v, g):
    L = q.shape[2]
    b = jnp.cumsum(g, axis=2)
    o_inter = jnp.einsum('bhld,bhde->bhle', q * jnp.exp(b), state)
    mask = jnp.tril(jnp.ones((L, L), dtype=bool))
    diff = b[:, :, :, None, :] - b[:, :, None, :, :]
    decay = jnp.exp(jnp.where(mask[:, :, None], diff, -jnp.inf))
    a = jnp.einsum('bhtd,bhsd,bhtsd->bhts', q, k, decay)
    o_intra = jnp.einsum('bhts,bhse->bhte', a, v)
    b_last = b[:, :, -1, :]
    new_state = jnp.exp(b_last)[..., None] * state + jnp.einsum('bhld,bhle->bhde', k * jnp.exp(b_last[:, :, None, :] - b), v)
    return new_state, o_inter + o_intra

def gla_output(o, g_out, norm_w, w_o, dtype):
    bsz, _, t, _ = o.shape
    o = o * lax.rsqrt(jnp.mean(o * o, axis=-1, keepdims=True) + NORM_EPS) * norm_w.astype(jnp.float32)
    o = o.transpose(0, 2, 1, 3).reshape(bsz, t, GLA_VALUE_DIM).astype(dtype)
    return (o * jax.nn.silu(g_out)) @ w_o

def gla_mix_prompt(h, w_in, w_gk2, b_gk, norm_w, w_o):
    bsz, t, _ = h.shape
    q, k, v, g, g_out = gla_project(h, w_in, w_gk2, b_gk)
    nc = t // CHUNK

    def to_chunks(a):
        return a.reshape(bsz, GLA_HEADS, nc, CHUNK, a.shape[-1]).transpose(2, 0, 1, 3, 4)

    def step(state, blk):
        return gla_chunk(state, *blk)

    s0 = jnp.zeros((bsz, GLA_HEADS, GLA_DK, GLA_DV), jnp.float32)
    s_final, o = lax.scan(step, s0, (to_chunks(q), to_chunks(k), to_chunks(v), to_chunks(g)))
    o = o.transpose(1, 2, 0, 3, 4).reshape(bsz, GLA_HEADS, t, GLA_DV)
    return gla_output(o, g_out, norm_w, w_o, h.dtype), s_final.astype(h.dtype)

def gla_mix_sample(h, state, w_in, w_gk2, b_gk, norm_w, w_o):
    q, k, v, g, g_out = gla_project(h, w_in, w_gk2, b_gk)
    s_new, o = gla_chunk(state.astype(jnp.float32), q, k, v, g)
    return gla_output(o, g_out, norm_w, w_o, h.dtype), s_new.astype(h.dtype)

def setup_inputs(seed: int = 0) -> dict:
    key = jax.random.key(seed)
    ks = jax.random.split(key, 24)
    f32 = jnp.float32

    def nrm(k, shape, scale=1.0):
        return jax.random.normal(k, shape, f32) * scale

    def w(k, shape, fan_in):
        return jax.random.normal(k, shape, f32) * (fan_in ** -0.5)

    def gain(k, shape):
        return 1.0 + 0.1 * jax.random.normal(k, shape, f32)

    return {
        'x_prompt': nrm(ks[0], (BATCH, SEQ, D_MODEL)),
        'x_sample': nrm(ks[1], (DEC_BATCH, DEC_SEQ, D_MODEL)),
        'cache_sb_k': nrm(ks[2], (N_SB, DEC_BATCH, PAST_LEN, SB_HEADS, SB_HEAD_DIM)),
        'cache_sb_v': nrm(ks[3], (N_SB, DEC_BATCH, PAST_LEN, SB_HEADS, SB_HEAD_DIM)),
        'state_conv': nrm(ks[4], (N_CONV, DEC_BATCH, CONV_WIDTH - 1, D_MODEL)),
        'state_gla': nrm(ks[5], (N_GLA, DEC_BATCH, GLA_HEADS, GLA_DK, GLA_DV), 0.5),
        'norm_mix': gain(ks[6], (DEPTH, D_MODEL)),
        'norm_mlp': gain(ks[7], (DEPTH, D_MODEL)),
        'sb_w_qkv': w(ks[8], (N_SB, D_MODEL, 3 * D_MODEL), D_MODEL),
        'sb_w_o': w(ks[9], (N_SB, D_MODEL, D_MODEL), D_MODEL),
        'conv_w_in': w(ks[10], (N_CONV, D_MODEL, 3 * D_MODEL), D_MODEL),
        'conv_w': w(ks[11], (N_CONV, CONV_WIDTH, D_MODEL), CONV_WIDTH),
        'conv_w_out': w(ks[12], (N_CONV, D_MODEL, D_MODEL), D_MODEL),
        'gla_w_in': w(ks[13], (N_GLA, D_MODEL, GLA_IN_DIM), D_MODEL),
        'gla_w_gk2': w(ks[14], (N_GLA, GLA_GATE_RANK, GLA_KEY_DIM), GLA_GATE_RANK),
        'gla_b_gk': nrm(ks[15], (N_GLA, GLA_KEY_DIM), 0.1),
        'gla_norm': gain(ks[16], (N_GLA, GLA_DV)),
        'gla_w_o': w(ks[17], (N_GLA, GLA_VALUE_DIM, D_MODEL), GLA_VALUE_DIM),
        'mlp_w_up': w(ks[18], (DEPTH, D_MODEL, MLP_HIDDEN), D_MODEL),
        'mlp_w_down': w(ks[19], (DEPTH, MLP_HIDDEN, D_MODEL), MLP_HIDDEN),
        'norm_final': gain(ks[20], (D_MODEL,)),
    }

def reference(x_prompt, x_sample, cache_sb_k, cache_sb_v, state_conv, state_gla,
              norm_mix, norm_mlp, sb_w_qkv, sb_w_o, conv_w_in, conv_w, conv_w_out,
              gla_w_in, gla_w_gk2, gla_b_gk, gla_norm, gla_w_o, mlp_w_up, mlp_w_down, norm_final):
    hp, hs = x_prompt, x_sample
    sb_k_p, sb_v_p, sb_k_s, sb_v_s = [], [], [], []
    conv_p, conv_s, gla_p, gla_s = [], [], [], []
    for i in range(DEPTH):
        j = i // N_MIXERS
        a_p = rms_norm(hp, norm_mix[i])
        a_s = rms_norm(hs, norm_mix[i])
        if i % N_MIXERS == 0:
            o_p, k_p, v_p = sb_mix_prompt(a_p, sb_w_qkv[j], sb_w_o[j])
            o_s, k_s, v_s = sb_mix_sample(a_s, cache_sb_k[j], cache_sb_v[j], sb_w_qkv[j], sb_w_o[j])
            sb_k_p.append(k_p); sb_v_p.append(v_p); sb_k_s.append(k_s); sb_v_s.append(v_s)
        elif i % N_MIXERS == 1:
            zero_prefix = jnp.zeros((a_p.shape[0], CONV_WIDTH - 1, D_MODEL), a_p.dtype)
            o_p, c_p = short_conv_mix(a_p, zero_prefix, conv_w_in[j], conv_w[j], conv_w_out[j])
            o_s, c_s = short_conv_mix(a_s, state_conv[j], conv_w_in[j], conv_w[j], conv_w_out[j])
            conv_p.append(c_p); conv_s.append(c_s)
        else:
            o_p, g_p = gla_mix_prompt(a_p, gla_w_in[j], gla_w_gk2[j], gla_b_gk[j], gla_norm[j], gla_w_o[j])
            o_s, g_s = gla_mix_sample(a_s, state_gla[j], gla_w_in[j], gla_w_gk2[j], gla_b_gk[j], gla_norm[j], gla_w_o[j])
            gla_p.append(g_p); gla_s.append(g_s)
        hp = hp + o_p
        hs = hs + o_s
        hp = hp + sq_relu_mlp(rms_norm(hp, norm_mlp[i]), mlp_w_up[i], mlp_w_down[i])
        hs = hs + sq_relu_mlp(rms_norm(hs, norm_mlp[i]), mlp_w_up[i], mlp_w_down[i])
    y_prompt = rms_norm(hp, norm_final)
    y_sample = rms_norm(hs, norm_final)
    return (y_prompt, y_sample,
            jnp.stack(sb_k_p), jnp.stack(sb_v_p), jnp.stack(sb_k_s), jnp.stack(sb_v_s),
            jnp.stack(conv_p), jnp.stack(conv_s), jnp.stack(gla_p), jnp.stack(gla_s))


_drawn_inputs = setup_inputs


def setup_inputs(seed=0):
    import zlib

    import numpy as np

    out = dict(_drawn_inputs(seed))
    spreads = {}
    factors = {}
    for name, (base, spread) in spreads.items():
        noise = np.random.default_rng([zlib.crc32(name.encode()), seed]).standard_normal(out[name].shape)
        drawn = base * np.exp(spread * noise) if base else spread * noise
        out[name] = __import__('jax').numpy.asarray(drawn.astype(out[name].dtype))
    for name, factor in factors.items():
        out[name] = (out[name] * factor).astype(out[name].dtype)
    return out
```

```python
from contextlib import ExitStack

import concourse.bass as bass
from concourse import mybir

F32 = mybir.dt.float32
F32R = mybir.dt.float32r
BF16 = mybir.dt.bfloat16
U8 = mybir.dt.uint8
ALU = mybir.AluOpType
ACT = mybir.ActivationFunctionType

P = 128
EPS = 1e-6
CLAMP = 2.0 ** 62
MASKED = -1e30
TRI = 8.0

D = 1024
KC = D // P
TP = 512
TS = 64
T = TP + TS
HALF = T // 2
NT = 5
SLAB = 256
HEADS = 16
HD = 64
PAST = 256

IN_SLABS = 3 * D // SLAB
OUT_SLABS = D // SLAB
GROUPS = 4
LAYER_SLABS = IN_SLABS + OUT_SLABS + GROUPS * 2 * OUT_SLABS
SLABS = 4 * LAYER_SLABS

V_MIX, V_MLP, V_FIN, V_CONV, V_BG, V_GN, V_STATE, V_ROWS = 0, 32, 64, 72, 96, 100, 102, 118

ZC = [0, 512, 1024, 1472]
COLS = 1472

GH = 4
GDK, GDV = 128, 256
GT = GH * T

TB_X, TB_VEC, TB_SB0, TB_GV, TB_GK, TB_SB3, TB_Y, TB_END = 0, 9, 10, 34, 44, 49, 73, 83
LEVELS = [0, 32, 16, 8, 4, 2, 1, 64]


def first_slab(layer):
    return layer * LAYER_SLABS


def batches_before(b, parity):
    return (b + 1 - parity) // 2


def trunk(nc, x_prompt, x_sample, cache_sb_k, cache_sb_v, state_conv, state_gla, norm_mix, norm_mlp, sb_w_qkv, sb_w_o,
          conv_w_in, conv_w, conv_w_out, gla_w_in, gla_w_gk2, gla_b_gk, gla_norm, gla_w_o, mlp_w_up, mlp_w_down,
          norm_final, y_prompt, y_sample, sb_k_p, sb_v_p, sb_k_s, sb_v_s, conv_p, conv_s, gla_p, gla_s):
    with ExitStack() as ctx:
        def sb(name, shape, dt):
            return ctx.enter_context(nc.sbuf_tensor(name, shape, dt))

        def sem(name):
            return ctx.enter_context(nc.semaphore(name))

        def passing(name, shape, dt):
            with nc.sbuf_tensor(name, shape, dt) as t:
                return t

        X = sb("X", [P, KC, T], F32)
        big = sb("big", [P, 3 * KC, T], F32)
        rstd = sb("rstd", [P, T], F32)
        vec = sb("vec", [P, V_ROWS], F32)
        ident = sb("ident", [P, P], F32)
        identb = sb("identb", [P, P], BF16)
        negones = sb("negones", [P, P], F32)
        negtri = sb("negtri", [P, P], F32)
        maskb = sb("maskb", [P, 192], BF16)
        zerob = sb("zerob", [P, TS], BF16)
        mask01 = sb("mask01", [P, 192], F32)
        lmask = sb("lmask", [P, 8, P], U8)
        rank_raw = sb("rank_raw", [P, KC, 16], F32)
        dec = sb("dec", [P, GH, NT], F32)
        rt, rt_m, rt_l = (sb(n, [P, NT], F32) for n in ("rt", "rt_m", "rt_l"))
        e2 = sb("e2", [P, COLS], F32)
        raw = sb("raw", [P, 2, KC, SLAB], F32)
        whi = sb("whi", [P, 2, KC, SLAB], F32R)
        wlo = sb("wlo", [P, 2, KC, SLAB], F32R)
        mixs = passing("mixs", [P, 9216], F32)
        ahi = sb("ahi", [P, KC, T], F32R)
        alo = sb("alo", [P, KC, T], F32R)
        stg = passing("stg", [P, 9216], F32)
        rankw = passing("rankw", [P, 2, KC, P], F32R)
        hhi = sb("hhi", [P, KC, T], F32R)
        hlo = sb("hlo", [P, KC, T], F32R)
        bank = [ctx.enter_context(nc.psum_tensor(f"bank{i}", [P, 512], F32)) for i in range(8)]

        def flat(a, b):
            return big[:, a:b, :].rearrange("p c t -> p (c t)")

        relu_t = [big[:, 16, :], big[:, 17, :]]
        sq_h = [big[:, 18, :], big[:, 19, :]]
        sq_x, ssq, ms, lt = (big[:, c, :] for c in (20, 21, 22, 23))

        slab_in = [sem("slab_in0"), sem("slab_in1")]
        w_hi = sem("w_hi")
        w_lo = sem("w_lo")
        chunk_done = sem("chunk_done")
        acc_free = sem("acc_free")
        sq_ready, ssq_add, xg_hi, xg_ready = sem("sq_ready"), sem("ssq_add"), sem("xg_hi"), sem("xg_ready")
        norm_sum, norm_v, norm_a = sem("norm_sum"), sem("norm_v"), sem("norm_a")
        hid_sq, hid_hi, hid_ready = sem("hid_sq"), sem("hid_hi"), sem("hid_ready")
        mix_hi, mix_ready = sem("mix_hi"), sem("mix_ready")
        x_in = [sem(f"x_in{i}") for i in range(NT)]
        vec_in, const_ready, pool_step = sem("vec_in"), sem("const_ready"), sem("pool_step")
        tp_ready, ev_v, ev_a = sem("tp_ready"), sem("ev_v"), sem("ev_a")
        ck_in, cv_in = sem("ck_in"), sem("cv_in")
        z_ready, e_ready, clamped, l_ready, sp_ready = (sem(n) for n in
                                                        ("z_ready", "e_ready", "clamped", "l_ready", "sp_ready"))
        sp_masked, carried, r_ready, a_ready, av_done = (sem(n) for n in
                                                         ("sp_masked", "carried", "r_ready", "a_ready", "av_done"))
        u_ready, y_ready, g_ready, conv_pre = sem("u_ready"), sem("y_ready"), sem("g_ready"), sem("conv_pre")
        rank_in, wgk_in, gs_in = sem("rank_in"), sem("wgk_in"), sem("gs_in")
        rank_z, rank_hi, rank_lo, rank_mm, gkl_ready, gk_mm = (sem(n) for n in
                                                               ("rank_z", "rank_hi", "rank_lo", "rank_mm",
                                                                "gkl_ready", "gk_mm"))
        reset_ready = sem("reset_ready")
        gv, ga, gp = sem("gv"), sem("ga"), sem("gp")
        gl_mm, gl_cp = sem("gl_mm"), sem("gl_cp")
        lv_d, lv_e, lv_q, lv_k = sem("lv_d"), sem("lv_e"), sem("lv_q"), sem("lv_k")
        o_mm, o_out, s_mm, s_new, gsum = sem("o_mm"), sem("o_out"), sem("s_mm"), sem("s_new"), sem("gsum")
        stored = sem("stored")
        kv_stored = sem("kv_stored")
        y_ev = sem("y_ev")

        def cols(w):
            return w.rearrange("(k p) c -> p k c", p=P)

        mix_in = [cols(sb_w_qkv[0]), cols(conv_w_in[0]), cols(gla_w_in[0]), cols(sb_w_qkv[1])]
        mix_out = [cols(sb_w_o[0]), cols(conv_w_out[0]), cols(gla_w_o[0]), cols(sb_w_o[1])]

        def slabs(eng, count, body, peeled=0):
            for s in range(peeled):
                body(s, s % 2)
            if peeled < count:
                with eng.Fori(0, (count - peeled) // 2) as i:
                    for u in range(2):
                        body(2 * i + (peeled + u), u)

        KT = stg[:, 0:5120].rearrange("p (t f) -> p t f", t=NT)
        CK = stg[:, 5120:7168].rearrange("p (j f) -> p j f", j=2)
        VT = mixs[:, 0:5120].rearrange("p (t f) -> p t f", t=NT)
        CV = mixs[:, 5120:7168].rearrange("p (j f) -> p j f", j=2)
        CKT = mixs[:, 7168:9216].rearrange("p (c k) -> p c k", c=KC)
        scr = flat(16, 24)
        ebuf = [scr[:, 0:COLS], scr[:, COLS:2 * COLS], e2[:, :]]
        carry = [scr[:, 2 * COLS:2 * COLS + 768], scr[:, 2 * COLS + 768:2 * COLS + 1536]]
        zbank = [bank[0:3], bank[3:6]]
        obank, osbank = bank[6], bank[7]

        U = mixs[:, 0:KC * 580].rearrange("p (c t) -> p c t", c=KC)
        Y = [mixs[:, 4640 + 580 * i:4640 + 580 * i + 578] for i in range(2)]
        Gt = [mixs[:, 5800 + 576 * i:5800 + 576 * i + 576] for i in range(2)]

        Cs = mixs[:, 5120:5120 + GT]
        Cs3 = Cs.rearrange("p (h t) -> p h t", h=GH)
        SS = mixs[:, 7424:8448].rearrange("p (h e) -> p h e", h=GH)
        qt, kt, dt_ = stg[:, 0:GT], stg[:, GT:2 * GT], stg[:, 2 * GT:3 * GT]
        d3 = dt_.rearrange("p (h t) -> p h t", h=GH)
        att = stg[:, 6912:8960].rearrange("p (h t) -> p h t", h=GH)
        ats = stg[0:TS, 8960:9216].rearrange("p (h t) -> p h t", h=GH)
        wgk = stg[0:16, 0:512]
        gkl = stg[0:16, 512:512 + T]
        reset = stg[:, 6912:6912 + T]
        KD_t = stg[:, 0:2560].rearrange("p (t f) -> p t f", t=NT)
        SP_ = stg[:, 2560:3584].rearrange("p (h e) -> p h e", h=GH)
        Q, K = flat(0, 4), flat(4, 8)
        QI, KD = flat(16 - 8, 16 - 4), flat(16 - 4, 16)
        O = big[:, 0:KC, :]
        SQ = big[:, 8:16, :]
        RG, rtmp = mixs[:, 0:GT], mixs[:, GT:2 * GT]
        RG3 = RG.rearrange("p (h t) -> p h t", h=GH)
        G = big[:, 16:24, :]

        def peel(count, norm, last):
            return count if last else 2 if norm is not None else 0

        block = ctx.enter_context(nc.Block())

        @block.sync
        def _(sp):
            for t in range(NT):
                src = x_prompt[0, t * P:(t + 1) * P, :] if t < 4 else x_sample[0]
                n = P if t < 4 else TS
                sp.dma_start(flat(0, 9)[0:n, t * D:(t + 1) * D], src).then_inc(x_in[t], 16)

            def load(base, w, count):
                def body(s, u):
                    sp.wait_ge(w_lo, base + s + 1)
                    sp.dma_start(raw[:, u], w[:, :, bass.ds(s * SLAB, SLAB)]).then_inc(slab_in[u], 16)
                slabs(sp, count, body)

            for layer in range(4):
                base = first_slab(layer)
                load(base, mix_in[layer], IN_SLABS)
                load(base + IN_SLABS, mix_out[layer], OUT_SLABS)
                for g in range(GROUPS):
                    b = base + IN_SLABS + OUT_SLABS + 2 * OUT_SLABS * g
                    load(b, cols(mlp_w_up[layer][:, g * D:(g + 1) * D]), OUT_SLABS)
                    load(b + OUT_SLABS, cols(mlp_w_down[layer][g * D:(g + 1) * D, :]), OUT_SLABS)

            sp.wait_ge(kv_stored, 16 * 8)
            sp.wait_ge(stored, 16 * STORES)

        @block.tensor
        def _(pe):
            pe.sem_inc(chunk_done, 3)

            def project(base, a_hi, a_lo, ready, ready_base, count, norm=None, unroll=False):
                def body(s, u):
                    pe.wait_ge(w_lo, base + s + 3)
                    for m in range(2):
                        acc = bank[4 * u + 2 * m:4 * u + 2 * m + 2]
                        pe.wait_ge(acc_free, 2 * (base + s) + m + 1)
                        if norm is not None and isinstance(s, int) and (s, m) == (1, 1):
                            pe.wait_ge(norm_v, 5 * norm + 1)
                        for k in range(KC):
                            if m == 0:
                                pe.wait_ge(ready, ready_base + k + 1)
                            for w, a in ((whi, a_hi), (whi, a_lo), (wlo, a_hi)):
                                for h in range(2):
                                    mm = pe.matmul(acc[h][:, 0:HALF], w[:, u, k, m * P:(m + 1) * P],
                                                   a[:, k, h * HALF:(h + 1) * HALF],
                                                   start=(k == 0 and w is whi and a is a_hi),
                                                   stop=(k == KC - 1 and w is wlo))
                        mm.then_inc(chunk_done, 1)
                        if norm is not None and isinstance(s, int) and (s, m) == (0, 0):
                            pe.wait_ge(acc_free, 2 * base + 4)
                            sum_squares(norm)
                slabs(pe, count, body, 2 if norm is not None else count if unroll else 0)

            def sum_squares(i):
                pe.wait_ge(ssq_add, 9 * (i + 1))
                for h in range(2):
                    mm = pe.matmul(bank[6 + h][:, 0:HALF], negones[:], ssq[:, h * HALF:(h + 1) * HALF],
                                   start=True, stop=True)
                mm.then_inc(norm_sum, 1)

            def bank_free(b):
                if b >= 8:
                    pe.wait_ge(ev_a if b % 2 else ev_v, (b - 8) // 2 + 1)

            pe.wait_ge(const_ready, CONSTS)
            x0 = flat(0, 9)
            for t in range(4):
                pe.wait_ge(x_in[t], 16)
                for c in range(KC):
                    mm = pe.transpose(bank[c][:, t * P:(t + 1) * P], x0[:, t * D + c * P:t * D + (c + 1) * P], ident[:])
                    if t == 3:
                        mm.then_inc(tp_ready, 1)
            pe.wait_ge(x_in[4], 16)
            bank_free(TB_X + 8)
            for c in range(KC):
                mm = pe.transpose(bank[0][:, c * TS:(c + 1) * TS], x0[0:TS, 4 * D + c * P:4 * D + (c + 1) * P],
                                  ident[0:TS, 0:TS])
            mm.then_inc(tp_ready, 1)
            pe.wait_ge(vec_in, 16 * VEC_DMAS)
            bank_free(TB_VEC)
            pe.transpose(bank[1][:, 0:V_ROWS], e2[0:V_ROWS, 0:P], ident[0:V_ROWS, 0:V_ROWS]).then_inc(tp_ready, 1)

            def wait_evacuated(b):
                pe.wait_ge(ev_v, batches_before(b, 0))
                pe.wait_ge(ev_a, batches_before(b, 1))

            def to_token_major(b0, src, first_chunk):
                for n in range(10):
                    t, g = n // 2, n % 2
                    b = b0 + n
                    bank_free(b)
                    w = P if t < 4 else TS
                    for c in range(4):
                        mm = pe.transpose(bank[b % 8][0:w, c * P:(c + 1) * P],
                                          src[:, first_chunk + 4 * g + c, t * P:t * P + w], ident[:])
                    mm.then_inc(tp_ready, 1)

            def stick_breaking(layer, sb_index):
                b0 = TB_SB0 if sb_index == 0 else TB_SB3
                pe.wait_ge(acc_free, 2 * (first_slab(layer) + IN_SLABS) + 4)
                to_token_major(b0, big, 16)
                pe.wait_ge(ck_in, 16 * (sb_index + 1))
                for n in range(4):
                    b = b0 + 10 + n
                    bank_free(b)
                    for i in range(4):
                        c, j = 2 * n + i // 2, i % 2
                        mm = pe.transpose(bank[b % 8][:, i * P:(i + 1) * P], CK[:, j, c * P:(c + 1) * P], ident[:])
                    mm.then_inc(tp_ready, 1)
                to_token_major(b0 + 14, big, 8)
                wait_evacuated(b0 + 24)
                first = HEADS * sb_index

                def scores(h):
                    p, r, z = h // 2, HD * (h % 2), zbank[h % 2]
                    H = first + h
                    if h >= 2:
                        pe.wait_ge(a_ready, 3 * (H - 1))
                    q = lambda lo, hi: big[r:r + HD, p, lo:hi]
                    key = lambda lo, hi: big[r:r + HD, 8 + p, lo:hi]
                    mmz = lambda b, lo, hi, kk, qq, start: pe.matmul(z[b][0:kk.shape[1], lo:hi], kk, qq, start=start,
                                                                     stop=False, skip_group_check=True)
                    mmz(0, 0, 512, key(0, 128), q(0, 512), True).then_inc(z_ready, 1)
                    mmz(1, 0, 384, key(128, 256), q(128, 512), True)
                    mmz(1, 384, 448, CKT[r:r + HD, p, 0:128], q(512, 576), False)
                    mmz(1, 448, 512, CKT[r:r + HD, p, 128:256], q(512, 576), False).then_inc(z_ready, 1)
                    mmz(2, 0, 256, key(256, 384), q(256, 512), True)
                    mmz(2, 256, 384, key(384, 512), q(384, 512), False)
                    mmz(2, 384, 448, identb[:], zerob[:], False)
                    mmz(2, 384, 448, key(512, 576), q(512, 576), False).then_inc(z_ready, 1)

                def cumulative(h):
                    z, s, cr = zbank[h % 2], ebuf[h % 3], carry[h % 2]
                    pe.wait_ge(sp_masked, first + h + 1)
                    acc = lambda b, lo, hi, w, m: pe.matmul(z[b][:, lo:hi], w, m, start=False, stop=False,
                                                            skip_group_check=True)
                    acc(0, 0, 512, negtri[:], s[:, 0:512])
                    acc(0, 0, 128, identb[:], maskb[:, 0:128])
                    acc(1, 0, 512, negtri[:], s[:, 512:1024])
                    acc(1, 0, 128, identb[:], maskb[:, 0:128])
                    acc(2, 0, 448, negtri[:], s[:, 1024:1472])
                    acc(2, 0, 128, identb[:], maskb[:, 0:128])
                    acc(2, 128, 256, negones[:], s[:, 1280:1408])
                    acc(2, 256, 448, identb[:], maskb[:]).then_inc(r_ready, 1)
                    pe.wait_ge(carried, first + h + 1)
                    acc(1, 128, 512, negones[:], cr[:, 384:768]).then_inc(r_ready, 1)
                    acc(0, 128, 512, negones[:], cr[:, 0:384]).then_inc(r_ready, 1)

                def weighted_values(h):
                    p, r, a = h // 2, HD * (h % 2), ebuf[h % 3]
                    hc = slice(h * HD, (h + 1) * HD)
                    pe.wait_ge(a_ready, 3 * (first + h) + 3)
                    if h == 0:
                        pe.wait_ge(cv_in, 16 * (sb_index + 1))
                    if h % 2 == 0 and h:
                        pe.wait_ge(mix_ready, 8 * layer + p)
                    av = lambda o, lo, hi, v, aa, start, stop: pe.matmul(o[r:r + HD, lo:hi], v, aa, start=start,
                                                                         stop=stop)
                    av(obank, 0, 512, VT[:, 0, hc], a[:, 0:512], True, False)
                    av(obank, 128, 512, VT[:, 1, hc], a[:, 512:896], False, False)
                    av(obank, 256, 512, VT[:, 2, hc], a[:, 1024:1280], False, False)
                    av(obank, 384, 512, VT[:, 3, hc], a[:, 1280:1408], False, True)
                    av(osbank, 0, TS, CV[:, 0, hc], a[:, 896:960], True, False)
                    av(osbank, 0, TS, CV[:, 1, hc], a[:, 960:1024], False, False)
                    av(osbank, 0, TS, VT[0:TS, 4, hc], a[0:TS, 1408:1472], False, True).then_inc(av_done, 1)

                scores(0)
                for h in range(HEADS):
                    if h + 1 < HEADS:
                        scores(h + 1)
                    if h:
                        weighted_values(h - 1)
                    cumulative(h)
                weighted_values(HEADS - 1)

            def linear_attention(layer):
                pe.wait_ge(rank_lo, 1)
                for k in range(KC):
                    for w, a in ((0, ahi), (0, alo), (1, ahi)):
                        for h in range(2):
                            mm = pe.matmul(bank[6 + h][:, 0:HALF], rankw[:, w, k, :], a[:, k, h * HALF:(h + 1) * HALF],
                                           start=(k == 0 and w == 0 and a is ahi), stop=(k == KC - 1 and w == 1))
                mm.then_inc(rank_mm, 1)
                pe.wait_ge(acc_free, 2 * (first_slab(layer) + IN_SLABS) + 4)
                pe.wait_ge(gkl_ready, 1)
                pe.wait_ge(wgk_in, 16)
                for c in range(GH):
                    for h in range(2):
                        mm = pe.matmul(bank[2 * c + h][:, 0:HALF], wgk[:, c * P:(c + 1) * P],
                                       gkl[:, h * HALF:(h + 1) * HALF], start=True, stop=True)
                    mm.then_inc(gk_mm, 1)
                pe.wait_ge(gv, 4)
                to_token_major(TB_GV, big, 8)
                wait_evacuated(TB_GV + 10)
                n = 0
                for li, half in enumerate(LEVELS):
                    if half == 0:
                        pe.wait_ge(gv, 11)
                    else:
                        pe.wait_ge(lv_q, li)
                        pe.wait_ge(lv_k, li)
                    qs, ks = (Q, K) if half == 0 else (qt, kt)
                    for h in range(GH + (half != 64)):
                        if n >= 8:
                            pe.wait_ge(gl_cp, n - 7)
                        b = bank[n % 8]
                        if h < GH:
                            for t in range(4):
                                cs = slice(h * T + t * P, h * T + (t + 1) * P)
                                mm = pe.matmul(b[:, t * P:(t + 1) * P], ks[:, cs], qs[:, cs], start=True, stop=True)
                        else:
                            for g in range(GH):
                                cs = slice(g * T + TP, (g + 1) * T)
                                mm = pe.matmul(b[0:TS, g * TS:(g + 1) * TS], ks[:, cs], qs[:, cs], start=True, stop=True)
                        mm.then_inc(gl_mm, 1)
                        n += 1
                pe.wait_ge(gl_cp, n)
                pe.wait_ge(gp, 3)
                for t in range(NT):
                    b = TB_GK + t
                    bank_free(b)
                    w = P if t < 4 else TS
                    for h in range(GH):
                        mm = pe.transpose(bank[b % 8][0:w, h * P:(h + 1) * P], KD[:, h * T + t * P:h * T + t * P + w],
                                          ident[:])
                    mm.then_inc(tp_ready, 1)
                wait_evacuated(TB_GK + 5)
                pe.wait_ge(gs_in, 16)
                for t in range(NT):
                    w = P if t < 4 else TS
                    bo = bank[0:2] if t % 2 == 0 else bank[4:6]
                    bs = bank[2:4] if t % 2 == 0 else bank[6:8]
                    state = SP_ if t < 4 else SS
                    if 0 < t < 4:
                        pe.wait_ge(s_new, 4 * t)
                    if t >= 2:
                        pe.wait_ge(o_out, t - 1)
                        pe.wait_ge(s_new, 4 * (t - 1))
                    for h in range(GH):
                        for j in range(2):
                            i = 2 * h + j
                            out = (bo[i // 4][:, (i % 4) * P:(i % 4) * P + P] if t < 4
                                   else bo[0][:, i * TS:(i + 1) * TS])
                            if t:
                                pe.matmul(out, state[:, h, j * P:(j + 1) * P], QI[:, h * T + t * P:h * T + t * P + w],
                                          start=True, stop=False)
                            a = att[:, h, t * P:(t + 1) * P] if t < 4 else ats[:, h, :]
                            mm = pe.matmul(out, VT[0:w, t, h * GDV + j * P:h * GDV + (j + 1) * P], a,
                                           start=(t == 0), stop=True)
                    mm.then_inc(o_mm, 1)
                    for h in range(GH):
                        mm = pe.matmul(bs[h // 2][:, (h % 2) * GDV:(h % 2 + 1) * GDV], KD_t[0:w, t, h * P:(h + 1) * P],
                                       VT[0:w, t, h * GDV:(h + 1) * GDV], start=True, stop=True)
                    mm.then_inc(s_mm, 1)
                pe.wait_ge(o_out, NT)
                pe.wait_ge(s_new, 4 * NT)
                pe.wait_ge(ga, GA_SQ)
                for h in range(GH):
                    for half in range(2):
                        for j in range(2):
                            mm = pe.matmul(bank[2 * h + half][:, 0:HALF], negones[:],
                                           SQ[:, 2 * h + j, half * HALF:(half + 1) * HALF], start=(j == 0), stop=(j == 1))
                    mm.then_inc(gsum, 1)

            for layer in range(4):
                base = first_slab(layer)
                project(base, ahi, alo, xg_ready, 16 * layer, IN_SLABS, norm=2 * layer)
                if layer in (0, 3):
                    stick_breaking(layer, layer // 3)
                elif layer == 2:
                    linear_attention(layer)
                project(base + IN_SLABS, hhi, hlo, mix_ready, 8 * layer, OUT_SLABS)
                for g in range(GROUPS):
                    b = base + IN_SLABS + OUT_SLABS + 2 * OUT_SLABS * g
                    project(b, ahi, alo, xg_ready, 16 * layer + 8, OUT_SLABS, norm=2 * layer + 1 if g == 0 else None)
                    project(b + OUT_SLABS, hhi, hlo, hid_ready, 8 * (GROUPS * layer + g), OUT_SLABS)
            pe.wait_ge(acc_free, 2 * SLABS + 4)
            pe.wait_ge(ssq_add, 9 * 9)
            for t in range(NT):
                w = P if t < 4 else TS
                mm = pe.matmul(bank[0][0:w, t:t + 1], ssq[:, t * P:t * P + w], negones[:, 0:1], start=True, stop=True)
            mm.then_inc(norm_sum, 1)
            pe.wait_ge(y_ev, 8)
            pe.wait_ge(norm_v, 5 * 8 + 1)
            to_token_major(TB_Y, big, 0)

        @block.scalar
        def _(act):
            act.preload_act_table_set("natural_log_exp_and_others")
            def split_next(base, s, u, half):
                n = base + s + 1
                act.wait_ge(slab_in[1 - u], 16 * (base // 2 + half + u) + 16)
                act.wait_ge(chunk_done, 2 * n + 1)
                act.activation(whi[:, 1 - u], raw[:, 1 - u], ACT.Copy).then_inc(w_hi, 1)

            def run(base, count, epilogue, norm=None, last=False):
                def body(s, u):
                    if isinstance(s, int):
                        if not (last and s == count - 1):
                            split_next(base, s, u, s // 2)
                        if s == 0 and norm is not None:
                            inverse_root(norm)
                        for m in range(2):
                            epilogue(s, m)
                for s in range(peel(count, norm, last)):
                    body(s, s % 2)
                if peel(count, norm, last) < count:
                    first = peel(count, norm, last)
                    with act.Fori(0, (count - first) // 2) as i:
                        for u in range(2):
                            split_next(base, 2 * i + (first + u), u, i + first // 2)
                            for m in range(2):
                                epilogue(2 * i + (first + u), m)

            def at(t, j):
                return t[:, j, :] if isinstance(j, int) else t[:, bass.ds(j, 1), :]

            def gained(i, j, gain):
                g = vec[:, gain + j:gain + j + 1] if isinstance(j, int) else vec[:, bass.ds(gain + j, 1)]
                act.activation(at(ahi, j), at(X, j), ACT.Copy, scale=g).then_inc(xg_hi, 1)

            def squared(i, j):
                act.activation(sq_x, at(X, j), ACT.Square).then_inc(sq_ready, 1)

            def inverse_root(i):
                act.wait_ge(norm_v, 5 * i + 1)
                act.activation(lt, ms, ACT.Ln).then_inc(norm_a, 1)
                act.wait_ge(norm_a, 2 * i + 1)
                act.activation(rstd[:], lt, ACT.Exp, scale=-0.5).then_inc(norm_a, 1)

            def nothing(s, m):
                pass

            def evacuate(b, dst, src):
                act.wait_ge(tp_ready, b + 1)
                act.activation(dst, src, ACT.Copy).then_inc(ev_a, 1)

            for c in range(1, KC, 2):
                evacuate(c, X[:, c, 0:TP], bank[c][:, :])
            evacuate(TB_VEC, vec[:], bank[1][:, 0:V_ROWS])
            act.wait_ge(ev_v, 5)
            act.wait_ge(ev_a, 5)
            act.wait_ge(slab_in[0], 16)
            act.activation(whi[:, 0], raw[:, 0], ACT.Copy).then_inc(w_hi, 1)
            for j in range(KC):
                gained(0, j, V_MIX)
            for j in range(KC):
                act.wait_ge(ssq_add, j + 1)
                squared(0, j)

            def token_major(b0, dst):
                for n in range(10):
                    b = b0 + n
                    if b % 2:
                        t, g = n // 2, n % 2
                        w = P if t < 4 else TS
                        evacuate(b, dst[0:w, t, g * 512:(g + 1) * 512], bank[b % 8][0:w, :])

            def stick_breaking(layer, sb_index):
                b0 = TB_SB0 if sb_index == 0 else TB_SB3
                token_major(b0, VT)
                for n in range(4):
                    b = b0 + 10 + n
                    if b % 2:
                        evacuate(b, CKT[:, 2 * n:2 * n + 2, :].rearrange("p c k -> p (c k)"), bank[b % 8][:, :])
                token_major(b0 + 14, KT)
                act.wait_ge(ev_v, batches_before(b0 + 24, 0))
                act.wait_ge(ev_a, batches_before(b0 + 24, 1))
                first = HEADS * sb_index

                def soft(h):
                    H = first + h
                    z, e = zbank[h % 2], ebuf[h % 3]
                    if h >= 3:
                        act.wait_ge(av_done, H - 2)
                    for b in range(3):
                        act.wait_ge(z_ready, 3 * H + b + 1)
                        act.activation(e[:, ZC[b]:ZC[b + 1]], z[b][:, 0:ZC[b + 1] - ZC[b]], ACT.Exp,
                                       scale=1 / TRI).then_inc(e_ready, 1)
                    act.wait_ge(clamped, H + 1)
                    act.activation(e, e, ACT.Ln, bias=1.0).then_inc(l_ready, 1)

                def weights(h):
                    H = first + h
                    z, e = zbank[h % 2], ebuf[h % 3]
                    act.wait_ge(carried, H + 1)
                    for n, b in enumerate((2, 1, 0)):
                        act.wait_ge(r_ready, 3 * H + (1, 2, 3)[n])
                        act.activation(e[:, ZC[b]:ZC[b + 1]], z[b][:, 0:ZC[b + 1] - ZC[b]], ACT.Exp,
                                       scale=1 / TRI).then_inc(a_ready, 1)

                def output(p):
                    act.wait_ge(av_done, first + 2 * p + 2)
                    if p == 0:
                        act.wait_ge(kv_stored, 16 * 4 * (sb_index + 1))
                    act.activation(hhi[:, p, 0:TP], obank[:, :], ACT.Copy)
                    act.activation(hhi[:, p, TP:T], osbank[:, 0:TS], ACT.Copy).then_inc(mix_hi, 1)

                soft(0)
                for h in range(HEADS):
                    if h + 1 < HEADS:
                        soft(h + 1)
                    if h % 2 == 0 and h:
                        output(h // 2 - 1)
                    weights(h)
                output(HEADS // 2 - 1)

            def convolution(layer):
                for c in range(KC):
                    act.wait_ge(g_ready, c + 1)
                    act.activation(hhi[:, c, :], Gt[c % 2], ACT.Copy).then_inc(mix_hi, 1)
                act.wait_ge(stored, 16 * 4)

            def linear_attention(layer):
                n = [0]

                def step(*args, **kw):
                    act.activation(*args, **kw).then_inc(ga, 1)
                    n[0] += 1

                act.wait_ge(gv, 4)
                step(dt_, Cs, ACT.Exp)
                act.wait_ge(gv, 5)
                step(dt_, dt_, ACT.Ln, bias=1.0)
                token_major(TB_GV, VT)
                act.wait_ge(gv, 10)
                act.wait_ge(ev_v, batches_before(TB_GV + 10, 0))
                act.wait_ge(ev_a, batches_before(TB_GV + 10, 1))
                step(QI, Cs, ACT.Exp, scale=-1 / 16)
                act.wait_ge(gp, 1)
                step(KD, KD, ACT.Exp, scale=1 / 16)
                ends = Cs3[:, :, 0:TP].rearrange("p h (t s) -> p h t s", t=4)[:, :, :, P - 1]
                step(dec[:, :, 0:4], ends, ACT.Exp, scale=-1 / 16)
                step(dec[:, :, 4:5], Cs3[:, :, T - 1:T], ACT.Exp, scale=-1 / 16)
                for li, half in enumerate(LEVELS):
                    if half:
                        act.wait_ge(lv_d, li)
                        d = d3[:, :, 0:TP] if half == 64 else dt_
                        act.activation(d, d, ACT.Exp, scale=1 / 16).then_inc(lv_e, 1)
                for t in range(NT):
                    b = TB_GK + t
                    if b % 2:
                        w = P if t < 4 else TS
                        evacuate(b, KD_t[0:w, t, :], bank[b % 8][0:w, :])
                for t in range(NT):
                    act.wait_ge(o_mm, t + 1)
                    bo = bank[0:2] if t % 2 == 0 else bank[4:6]
                    if t < 4:
                        for g in range(2):
                            mm = act.activation(O[:, 4 * g:4 * g + 4, t * P:(t + 1) * P],
                                                bo[g][:, :].rearrange("p (c t) -> p c t", c=4), ACT.Copy)
                    else:
                        mm = act.activation(O[:, :, TP:T], bo[0][:, :].rearrange("p (c t) -> p c t", c=8), ACT.Copy)
                    mm.then_inc(o_out, 1)
                act.wait_ge(o_out, NT)
                step(SQ[:, :, :], O[:, :, :], ACT.Square)
                assert n[0] == GA_SQ
                act.wait_ge(gv, GV_MS)
                step(RG, Cs, ACT.Ln)
                act.wait_ge(ga, GA_SQ + 1)
                step(RG, RG, ACT.Exp, scale=-0.5)
                act.wait_ge(gsum, GH)
                step(SQ[:, :, :], G[:, :, :], ACT.Exp, scale=-1.0)
                act.wait_ge(stored, 16 * 6)
                for c in range(KC):
                    act.wait_ge(g_ready, KC + c + 1)
                    act.activation(hhi[:, c, :], O[:, c, :], ACT.Copy).then_inc(mix_hi, 1)

            for layer in range(4):
                base = first_slab(layer)
                run(base, IN_SLABS, nothing, norm=2 * layer)
                (stick_breaking if layer in (0, 3) else convolution if layer == 1 else linear_attention)(
                    *((layer, layer // 3) if layer in (0, 3) else (layer,)))

                def residual(b, i, gain):
                    def epilogue(s, m):
                        act.wait_ge(ssq_add, 9 * i + 2 * s + m + 1)
                        act.wait_ge(acc_free, 2 * (b + s) + m + 5)
                        if gain is not None:
                            gained(i, 2 * s + m, gain)
                        squared(i, 2 * s + m)
                    return epilogue

                def hidden(b, g):
                    def epilogue(s, m):
                        act.wait_ge(acc_free, 2 * (b + s) + m + 5)
                        c = 2 * s + m
                        act.activation(sq_h[m], relu_t[m], ACT.Square).then_inc(hid_sq, 1)
                        act.activation(at(hhi, c), relu_t[m], ACT.Square).then_inc(hid_hi, 1)
                    return epilogue

                b = base + IN_SLABS
                run(b, OUT_SLABS, residual(b, 2 * layer + 1, V_MLP + 8 * layer))
                for g in range(GROUPS):
                    b = base + IN_SLABS + OUT_SLABS + 2 * OUT_SLABS * g
                    run(b, OUT_SLABS, hidden(b, g), norm=2 * layer + 1 if g == 0 else None)
                    last = g == GROUPS - 1
                    gain = V_MIX + 8 * (layer + 1) if layer < 3 else None
                    b += OUT_SLABS
                    run(b, OUT_SLABS, residual(b, 2 * layer + 2, gain) if last else nothing, last=last and layer == 3)

            act.wait_ge(norm_v, 5 * 8 + 1)
            act.activation(rt_l[:], rt_m[:], ACT.Ln).then_inc(norm_a, 1)
            act.wait_ge(norm_a, 2 * 8 + 1)
            act.activation(rt[:], rt_l[:], ACT.Exp, scale=-0.5).then_inc(norm_a, 1)
            act.wait_ge(norm_v, 5 * 8 + 5)
            for n in range((TB_Y + 1) % 2, 10, 2):
                t, g = n // 2, n % 2
                w = P if t < 4 else TS
                act.wait_ge(tp_ready, TB_Y + n + 1)
                act.activation(VT[0:w, t, g * 512:(g + 1) * 512], bank[(TB_Y + n) % 8][0:w, :], ACT.Copy,
                               scale=rt[0:w, t:t + 1]).then_inc(ev_a, 1)

        @block.vector
        def _(dve):
            dve.sem_inc(w_lo, 2)
            dve.sem_inc(acc_free, 4)

            def split(n, u):
                dve.wait_ge(w_hi, n + 1)
                dve.tensor_tensor(wlo[:, u], raw[:, u], whi[:, u].bitcast(F32), ALU.subtract).then_inc(w_lo, 1)

            def run(base, count, epilogue, norm=None, last=False):
                def body(s, u):
                    if not (last and s == count - 1):
                        split(base + s + 1, 1 - u)
                    if norm is not None and isinstance(s, int) and s == 0:
                        inverse_root(norm)
                    for m in range(2):
                        dve.wait_ge(chunk_done, 2 * (base + s) + m + 4)
                        epilogue(s, u, m)
                slabs(dve, count, body, peel(count, norm, last))

            def at(t, j):
                return t[:, j, :] if isinstance(j, int) else t[:, bass.ds(j, 1), :]

            def part(t, j, cols_):
                return t[:, j, cols_] if isinstance(j, int) else t[:, bass.ds(j, 1), cols_]

            def normed(i, j, gain):
                dve.wait_ge(xg_hi, 8 * i + j + 1)
                g = vec[:, gain + j:gain + j + 1] if isinstance(j, int) else vec[:, bass.ds(gain + j, 1)]
                dve.scalar_tensor_tensor(at(alo, j), at(X, j), g, at(ahi, j).bitcast(F32), ALU.mult,
                                         ALU.subtract).then_inc(xg_ready, 1)

            def refine(y, mean, tmp, done, before):
                dve.tensor_tensor(tmp, y, y, ALU.mult).then_inc(done, 1)
                dve.wait_ge(done, before + 1)
                dve.tensor_tensor(tmp, tmp, mean, ALU.mult).then_inc(done, 1)
                dve.wait_ge(done, before + 2)
                dve.tensor_scalar(tmp, tmp, -0.5, 1.5, ALU.mult, ALU.add).then_inc(done, 1)
                dve.wait_ge(done, before + 3)
                dve.tensor_tensor(y, y, tmp, ALU.mult).then_inc(done, 1)

            def inverse_root(i):
                dve.wait_ge(norm_sum, i + 1)
                for h in range(2):
                    ins = dve.tensor_scalar(ms[:, h * HALF:(h + 1) * HALF], bank[6 + h][:, 0:HALF], -1 / (TRI * D), EPS,
                                            ALU.mult, ALU.add)
                ins.then_inc(norm_v, 1)
                dve.wait_ge(norm_a, 2 * i + 2)
                refine(rstd[:], ms, lt, norm_v, 5 * i + 1)
                dve.wait_ge(norm_v, 5 * i + 5)

            def evacuate(b, dst, src):
                dve.wait_ge(tp_ready, b + 1)
                dve.tensor_copy(dst, src).then_inc(ev_v, 1)

            def token_major(b0, dst):
                for n in range(10):
                    b = b0 + n
                    if b % 2 == 0:
                        t, g = n // 2, n % 2
                        w = P if t < 4 else TS
                        evacuate(b, dst[0:w, t, g * 512:(g + 1) * 512], bank[b % 8][0:w, :])

            for c in range(0, KC, 2):
                evacuate(c, X[:, c, 0:TP], bank[c][:, :])
            evacuate(8, X[:, :, TP:T], bank[0][:, :].rearrange("p (c t) -> p c t", c=KC))
            split(0, 0)
            for j in range(KC):
                normed(0, j, V_MIX)

            def project_out(s, u, m):
                for h in range(2):
                    hs = slice(h * HALF, (h + 1) * HALF)
                    ins = dve.tensor_tensor(part(big, 2 * s + m, hs), bank[4 * u + 2 * m + h][:, 0:HALF], rstd[:, hs],
                                            ALU.mult)
                ins.then_inc(acc_free, 1)

            def stick_breaking(layer, sb_index):
                b0 = TB_SB0 if sb_index == 0 else TB_SB3
                token_major(b0, VT)
                for n in range(4):
                    b = b0 + 10 + n
                    if b % 2 == 0:
                        evacuate(b, CKT[:, 2 * n:2 * n + 2, :].rearrange("p c k -> p (c k)"), bank[b % 8][:, :])
                token_major(b0 + 14, KT)
                first = HEADS * sb_index

                def softplus(h):
                    H = first + h
                    z, e = zbank[h % 2], ebuf[h % 3]
                    dve.wait_ge(e_ready, 3 * H + 3)
                    dve.tensor_scalar(e, e, CLAMP, None, ALU.min).then_inc(clamped, 1)
                    dve.wait_ge(l_ready, H + 1)
                    for b in range(3):
                        cs = slice(ZC[b], ZC[b + 1])
                        ins = dve.scalar_tensor_tensor(e[:, cs], z[b][:, 0:ZC[b + 1] - ZC[b]], 1 / TRI, e[:, cs],
                                                       ALU.mult, ALU.max)
                    ins.then_inc(sp_ready, 1)

                def output(p):
                    dve.wait_ge(mix_hi, 8 * layer + p + 1)
                    dve.tensor_tensor(hlo[:, p, 0:TP], obank[:, :], hhi[:, p, 0:TP].bitcast(F32), ALU.subtract)
                    dve.tensor_tensor(hlo[:, p, TP:T], osbank[:, 0:TS], hhi[:, p, TP:T].bitcast(F32),
                                      ALU.subtract).then_inc(mix_ready, 1)

                softplus(0)
                for h in range(HEADS):
                    if h + 1 < HEADS:
                        softplus(h + 1)
                    if h % 2 == 0 and h:
                        output(h // 2 - 1)
                output(HEADS // 2 - 1)

            def convolution(layer):
                for c in range(KC):
                    y = Y[c % 2]
                    w = [vec[:, V_CONV + 8 * i + c:V_CONV + 8 * i + c + 1] for i in range(3)]
                    dve.wait_ge(u_ready, c + 1)
                    if c >= 2:
                        dve.wait_ge(g_ready, c - 1)
                    dve.tensor_scalar(y, U[:, c, 0:578], w[0], None, ALU.mult).then_inc(y_ready, 1)
                    for i in (1, 2):
                        dve.wait_ge(y_ready, 3 * c + i)
                        dve.scalar_tensor_tensor(y, U[:, c, i:578 + i], w[i], y, ALU.mult, ALU.add).then_inc(y_ready, 1)
                    if c:
                        lo_part(layer, c - 1, Gt[(c - 1) % 2])
                lo_part(layer, KC - 1, Gt[(KC - 1) % 2])

            def lo_part(layer, c, src):
                dve.wait_ge(mix_hi, 8 * layer + c + 1)
                dve.tensor_tensor(hlo[:, c, :], src, hhi[:, c, :].bitcast(F32), ALU.subtract).then_inc(mix_ready, 1)

            def linear_attention(layer):
                dve.wait_ge(rank_hi, 1)
                dve.tensor_tensor(rankw[:, 1, :, 0:16], rank_raw[:], rankw[:, 0, :, 0:16].bitcast(F32),
                                  ALU.subtract).then_inc(rank_lo, 1)
                dve.wait_ge(rank_mm, 1)
                for h in range(2):
                    hs = slice(h * HALF, (h + 1) * HALF)
                    ins = dve.tensor_tensor(gkl[:, hs], bank[6 + h][0:16, 0:HALF], rstd[0:16, hs], ALU.mult)
                ins.then_inc(gkl_ready, 1)
                for c in range(GH):
                    dve.wait_ge(gk_mm, c + 1)
                    for h in range(2):
                        ins = dve.tensor_scalar(Cs3[:, c, h * HALF:(h + 1) * HALF], bank[2 * c + h][:, 0:HALF], -1.0,
                                                vec[:, V_BG + c:V_BG + c + 1], ALU.mult, ALU.subtract)
                    ins.then_inc(gv, 1)
                dve.wait_ge(ga, 1)
                dve.tensor_scalar(dt_, dt_, CLAMP, None, ALU.min).then_inc(gv, 1)
                token_major(TB_GV, VT)
                dve.wait_ge(ga, 2)
                dve.tensor_tensor(dt_, dt_, Cs, ALU.max).then_inc(gv, 1)
                dve.wait_ge(gv, 6)
                dve.wait_ge(reset_ready, 1)
                for h in range(GH):
                    dve.tensor_tensor_scan(Cs3[:, h, :], reset, d3[:, h, :], 0.0, ALU.mult, ALU.add).then_inc(gv, 1)
                dve.tensor_scalar(Q, Q, float(GDK) ** -0.5, None, ALU.mult).then_inc(gv, 1)
                dve.wait_ge(gv, 11)
                n = 0
                for li, half in enumerate(LEVELS):
                    if half:
                        if li > 1:
                            dve.wait_ge(lv_q, li - 1)
                            dve.wait_ge(lv_k, li - 1)
                        if half == 64:
                            for h in range(GH):
                                c4 = Cs3[:, h, 0:TP].rearrange("p (b s) -> p b s", s=P)
                                dd = d3[:, h, 0:TP].rearrange("p (b s) -> p b s", s=P)
                                mid = c4[:, :, 63:64].to_broadcast([P, 4, 64])
                                dve.tensor_tensor(dd[:, :, 0:64], c4[:, :, 0:64], mid, ALU.subtract)
                                ins = dve.tensor_tensor(dd[:, :, 64:P], mid, c4[:, :, 64:P], ALU.subtract)
                        else:
                            c4 = Cs.rearrange("p (b s) -> p b s", s=2 * half)
                            dd = dt_.rearrange("p (b s) -> p b s", s=2 * half)
                            mid = c4[:, :, half - 1:half].to_broadcast([P, GT // (2 * half), half])
                            dve.tensor_tensor(dd[:, :, 0:half], c4[:, :, 0:half], mid, ALU.subtract)
                            ins = dve.tensor_tensor(dd[:, :, half:2 * half], mid, c4[:, :, half:2 * half], ALU.subtract)
                        ins.then_inc(lv_d, 1)
                        dve.wait_ge(lv_e, li)
                        dve.wait_ge(gl_mm, n)
                        if half == 64:
                            q3, s3 = (t.rearrange("p (h t) -> p h t", h=GH)[:, :, 0:TP] for t in (qt, Q))
                            dve.tensor_tensor(q3, s3, d3[:, :, 0:TP], ALU.mult).then_inc(lv_q, 1)
                        else:
                            dve.tensor_tensor(qt, Q, dt_, ALU.mult).then_inc(lv_q, 1)
                    mask = ident if half == 0 else lmask
                    for h in range(GH + (half != 64)):
                        dve.wait_ge(gl_mm, n + 1)
                        b = bank[n % 8]
                        if h < GH:
                            a, src = att[:, h, :].rearrange("p (t s) -> p t s", t=4), b[:, :].rearrange("p (t s) -> p t s", t=4)
                            rows, w, reps = P, P, 4
                        else:
                            a, src = ats[:, :, :], b[0:TS, 0:GH * TS].rearrange("p (t s) -> p t s", t=GH)
                            rows, w, reps = TS, TS, GH
                        if half == 0:
                            m = ident[0:rows, 0:w].unsqueeze(1).to_broadcast([rows, reps, w])
                            dve.tensor_tensor(a, src, m, ALU.mult).then_inc(gl_cp, 1)
                        else:
                            m = lmask[0:rows, li, 0:w].unsqueeze(1).to_broadcast([rows, reps, w])
                            dve.wait_ge(gl_cp, n)
                            dve.copy_predicated(a, m, src).then_inc(gl_cp, 1)
                        n += 1
                dve.wait_ge(gl_mm, n)
                for t in range(NT):
                    b = TB_GK + t
                    if b % 2 == 0:
                        w = P if t < 4 else TS
                        evacuate(b, KD_t[0:w, t, :], bank[b % 8][0:w, :])
                for t in range(NT):
                    bs = bank[2:4] if t % 2 == 0 else bank[6:8]
                    dve.wait_ge(s_mm, t + 1)
                    if t:
                        dve.wait_ge(s_new, 4 * t)
                    for h in range(GH):
                        src = bs[h // 2][:, (h % 2) * GDV:(h % 2 + 1) * GDV]
                        if t == 0:
                            dve.tensor_copy(SP_[:, h, :], src).then_inc(s_new, 1)
                        else:
                            s = SP_ if t < 4 else SS
                            dve.scalar_tensor_tensor(s[:, h, :], s[:, h, :], dec[:, h, t:t + 1], src, ALU.mult,
                                                     ALU.add).then_inc(s_new, 1)
                for h in range(GH):
                    dve.wait_ge(gsum, h + 1)
                    for half in range(2):
                        ins = dve.tensor_scalar(Cs3[:, h, half * HALF:(half + 1) * HALF], bank[2 * h + half][:, 0:HALF],
                                                -1 / (TRI * GDV), EPS, ALU.mult, ALU.add)
                    ins.then_inc(gv, 1)
                dve.wait_ge(ga, GA_SQ + 2)
                refine(RG, Cs, rtmp, gv, GV_MS)
                dve.wait_ge(ga, GA_SQ + 3)
                dve.wait_ge(gv, GV_MS + 4)
                dve.tensor_scalar(SQ[:, :, :], SQ[:, :, :], 1.0, None, ALU.add).then_inc(gv, 1)
                dve.wait_ge(gv, GV_MS + 5)
                dve.reciprocal(SQ[:, :, :], SQ[:, :, :]).then_inc(gv, 1)
                for c in range(KC):
                    w = vec[:, V_GN + c % 2:V_GN + c % 2 + 1]
                    dve.scalar_tensor_tensor(O[:, c, :], O[:, c, :], w, RG3[:, c // 2, :], ALU.mult,
                                             ALU.mult).then_inc(gv, 1)
                    if c:
                        lo_part(layer, c - 1, O[:, c - 1, :])
                lo_part(layer, KC - 1, O[:, KC - 1, :])

            for layer in range(4):
                base = first_slab(layer)
                run(base, IN_SLABS, project_out, norm=2 * layer)
                if layer in (0, 3):
                    stick_breaking(layer, layer // 3)
                elif layer == 1:
                    convolution(layer)
                else:
                    linear_attention(layer)

                def residual(b, i, gain):
                    def epilogue(s, u, m):
                        j = 2 * s + m
                        for h in range(2):
                            hs = slice(h * HALF, (h + 1) * HALF)
                            ins = dve.tensor_tensor(part(X, j, hs), bank[4 * u + 2 * m + h][:, 0:HALF], part(X, j, hs),
                                                    ALU.add)
                        ins.then_inc(acc_free, 1)
                        if gain == V_FIN:
                            dve.wait_ge(acc_free, 2 * (b + s) + m + 5)
                            dve.tensor_scalar(at(big, j), at(X, j), vec[:, gain + j:gain + j + 1], None,
                                              ALU.mult).then_inc(y_ev, 1)
                        elif gain is not None:
                            normed(i, j, gain)
                    return epilogue

                def hidden(b, g):
                    def epilogue(s, u, m):
                        c = 2 * s + m
                        n = 8 * (GROUPS * layer + g)
                        for h in range(2):
                            hs = slice(h * HALF, (h + 1) * HALF)
                            ins = dve.scalar_tensor_tensor(relu_t[m][:, hs], bank[4 * u + 2 * m + h][:, 0:HALF], 0.0, rstd[:, hs],
                                                           ALU.max, ALU.mult)
                        ins.then_inc(acc_free, 1)
                        dve.wait_ge(hid_hi, n + c + 1)
                        dve.tensor_tensor(at(hlo, c), sq_h[m], at(hhi, c).bitcast(F32),
                                          ALU.subtract).then_inc(hid_ready, 1)
                    return epilogue

                b = base + IN_SLABS
                run(b, OUT_SLABS, residual(b, 2 * layer + 1, V_MLP + 8 * layer))
                for g in range(GROUPS):
                    b = base + IN_SLABS + OUT_SLABS + 2 * OUT_SLABS * g
                    run(b, OUT_SLABS, hidden(b, g), norm=2 * layer + 1 if g == 0 else None)
                    b += OUT_SLABS
                    last = g == GROUPS - 1
                    gain = None if not last else V_MIX + 8 * (layer + 1) if layer < 3 else V_FIN
                    run(b, OUT_SLABS, residual(b, 2 * layer + 2, gain), last=last and layer == 3)

            dve.wait_ge(norm_sum, 9)
            dve.memset(rt_m[:], 1.0).then_inc(y_ev, 1)
            dve.wait_ge(y_ev, 9)
            dve.tensor_scalar(rt_m[:, 0:4], bank[0][:, 0:4], -1 / (TRI * D), EPS, ALU.mult, ALU.add)
            dve.tensor_scalar(rt_m[0:TS, 4:5], bank[0][0:TS, 4:5], -1 / (TRI * D), EPS, ALU.mult,
                              ALU.add).then_inc(norm_v, 1)
            dve.wait_ge(norm_a, 2 * 8 + 2)
            refine(rt[:], rt_m[:], rt_l[:], norm_v, 5 * 8 + 1)
            dve.wait_ge(norm_v, 5 * 8 + 5)
            for n in range((TB_Y + 0) % 2, 10, 2):
                t, g = n // 2, n % 2
                w = P if t < 4 else TS
                dve.wait_ge(tp_ready, TB_Y + n + 1)
                dve.tensor_scalar(VT[0:w, t, g * 512:(g + 1) * 512], bank[(TB_Y + n) % 8][0:w, :], rt[0:w, t:t + 1],
                                  None, ALU.mult).then_inc(ev_v, 1)

        @block.gpsimd
        def _(pool):
            row = 0
            for src, n in ((norm_mix.rearrange("l (c p) -> (l c) p", p=P), 32),
                           (norm_mlp.rearrange("l (c p) -> (l c) p", p=P), 32),
                           (norm_final.rearrange("(c p) -> c p", p=P), 8),
                           (conv_w[0].rearrange("i (c p) -> (i c) p", p=P), 24),
                           (gla_b_gk[0].rearrange("(c p) -> c p", p=P), 4),
                           (gla_norm[0].rearrange("(c p) -> c p", p=P), 2),
                           (state_conv[0, 0].rearrange("i (c p) -> (i c) p", p=P), 16)):
                pool.dma_start(e2[row:row + n, 0:P], src).then_inc(vec_in, 16)
                row += n
            pool.dma_start(rank_raw[:], gla_w_in[0].rearrange("(k p) c -> p k c", p=P)[:, :, 3 * D:3 * D + 16])\
                .then_inc(rank_in, 16)
            pool.dma_start(CK, cache_sb_k[0, 0].rearrange("(j p) h d -> p j (h d)", p=P)).then_inc(ck_in, 16)

            steps = [0]

            def made(ins):
                ins.then_inc(pool_step, 1)
                steps[0] += 1
                pool.wait_ge(pool_step, steps[0])

            made(pool.memset(ident[:], 0.0))
            pool.affine_select(ident[:], ident[:], [[-1, P]], ALU.not_equal, 1.0, base=0,
                               channel_multiplier=1).then_inc(const_ready, 1)
            pool.memset(negones[:], -TRI).then_inc(const_ready, 1)
            made(pool.memset(negtri[:], -TRI))
            pool.affine_select(negtri[:], negtri[:], [[-1, P]], ALU.is_ge, 0.0, base=0,
                               channel_multiplier=1).then_inc(const_ready, 1)
            pool.memset(zerob[:], 0.0).then_inc(const_ready, 1)
            made(pool.memset(mask01[:], 1.0))
            for lo, hi in ((0, P), (P, 192)):
                made(pool.affine_select(mask01[:, lo:hi], mask01[:, lo:hi], [[1, hi - lo]], ALU.is_gt, 0.0, base=0,
                                        channel_multiplier=-1))
            pool.tensor_scalar(maskb[:], mask01[:], 1.0, -MASKED, ALU.subtract, ALU.mult).then_inc(const_ready, 1)
            pool.wait_ge(const_ready, 5)
            pool.tensor_copy(identb[:], ident[:]).then_inc(const_ready, 1)
            def at(t, j):
                return t[:, j, :] if isinstance(j, int) else t[:, bass.ds(j, 1), :]

            def add_squares(i):
                pool.memset(ssq, 0.0).then_inc(ssq_add, 1)
                with pool.Fori(0, KC) as j:
                    pool.wait_ge(ssq_add, 9 * i + 1 + j)
                    pool.wait_ge(sq_ready, 8 * i + 1 + j)
                    pool.tensor_tensor(ssq, ssq, sq_x, ALU.add).then_inc(ssq_add, 1)

            add_squares(0)

            lm = stg[:, 8192:8192 + P]
            for li, half in enumerate(LEVELS):
                if half:
                    made(pool.memset(lm, 1.0))
                    v = lm.rearrange("p (b s) -> p b s", s=2 * half)
                    nb = P // (2 * half)
                    for pattern, base, ch in (([[-2 * half, nb], [0, 2 * half]], 0, 1),
                                              ([[2 * half, nb], [0, 2 * half]], half - 1, -1),
                                              ([[0, nb], [1, 2 * half]], -half, 0)):
                        made(pool.affine_select(v, v, pattern, ALU.is_ge, 0.0, base=base, channel_multiplier=ch))
                    made(pool.tensor_copy(lmask[:, li, :], lm))

            def stick_breaking(layer, sb_index):
                first = HEADS * sb_index
                b0 = TB_SB0 if sb_index == 0 else TB_SB3
                pool.wait_ge(chunk_done, 2 * (first_slab(layer) + IN_SLABS) + 3)
                pool.dma_start(CV, cache_sb_v[sb_index, 0].rearrange("(j p) h d -> p j (h d)", p=P)).then_inc(cv_in, 16)
                pool.wait_ge(ev_v, batches_before(b0 + 24, 0))
                pool.wait_ge(ev_a, batches_before(b0 + 24, 1))
                for src, d_p, d_s in ((KT, sb_k_p, sb_k_s), (VT, sb_v_p, sb_v_s)):
                    pool.dma_start(d_p[sb_index, 0].rearrange("(t p) h d -> p t (h d)", p=P),
                                   src[:, 0:4, :]).then_inc(kv_stored, 16)
                    pool.dma_start(d_s[sb_index, 0].rearrange("p h d -> p (h d)"), src[0:TS, 4, :]).then_inc(kv_stored, 16)
                for h in range(HEADS):
                    H = first + h
                    s, cr = ebuf[h % 3], carry[h % 2]
                    pool.wait_ge(sp_ready, H + 1)
                    if h >= 2:
                        pool.wait_ge(r_ready, 3 * (H - 1))
                    for lo in (0, 512, 1024):
                        pool.tensor_tensor(s[:, lo:lo + P], s[:, lo:lo + P], mask01[:, 0:P], ALU.mult)
                    pool.tensor_tensor(s[:, 1280:1472], s[:, 1280:1472], mask01[:], ALU.mult).then_inc(sp_masked, 1)
                    pool.wait_ge(sp_masked, H + 1)
                    made(pool.tensor_tensor(cr[:, 512:640], s[:, 1152:1280], s[:, 1280:1408], ALU.add))
                    pool.tensor_copy(cr[:, 384:512], s[:, 1024:1152])
                    pool.tensor_tensor(cr[:, 640:704], s[:, 960:1024], s[:, 1408:1472], ALU.add)
                    made(pool.tensor_copy(cr[:, 704:768], s[:, 1408:1472]))
                    pool.tensor_copy(cr[:, 0:128], s[:, 512:640])
                    pool.tensor_tensor(cr[:, 128:384], s[:, 640:896], cr[:, 384:640], ALU.add).then_inc(carried, 1)

            def convolution(layer):
                pool.wait_ge(chunk_done, 2 * (first_slab(layer) + IN_SLABS) + 3)
                pool.memset(U[:, :, 0:2], 0.0)
                made(pool.tensor_copy(U[:, :, 514:516],
                                      vec[:, V_STATE:V_STATE + 16].rearrange("p (i c) -> p c i", i=2)))
                pool.wait_ge(acc_free, 2 * (first_slab(layer) + IN_SLABS) + 4)

                def gate(c):
                    g, y = Gt[c % 2], Y[c % 2]
                    pool.wait_ge(y_ready, 3 * c + 3)
                    if c >= 2:
                        pool.wait_ge(mix_ready, 8 * layer + c - 1)
                    pool.tensor_tensor(g[:, 0:TP], y[:, 0:TP], big[:, c, 0:TP], ALU.mult)
                    pool.tensor_tensor(g[:, TP:T], y[:, 514:578], big[:, c, TP:T], ALU.mult).then_inc(g_ready, 1)

                for c in range(KC):
                    pool.tensor_tensor(U[:, c, 2:514], big[:, 8 + c, 0:TP], big[:, 16 + c, 0:TP], ALU.mult)
                    pool.tensor_tensor(U[:, c, 516:580], big[:, 8 + c, TP:T], big[:, 16 + c, TP:T],
                                       ALU.mult).then_inc(u_ready, 1)
                    if c:
                        gate(c - 1)
                gate(KC - 1)
                pool.wait_ge(u_ready, KC)
                for i in range(2):
                    for dst, at_ in ((conv_p, 512), (conv_s, 578)):
                        pool.dma_start(dst[0, 0, i].rearrange("(c p) -> p c", p=P).unsqueeze(2),
                                       U[:, :, at_ + i:at_ + i + 1], allow_slow_non_contiguous=True).then_inc(stored, 16)

            def linear_attention(layer):
                pool.wait_ge(gv, 10)
                pool.wait_ge(ev_v, batches_before(TB_GV + 10, 0))
                pool.wait_ge(ev_a, batches_before(TB_GV + 10, 1))
                for h in range(GH):
                    kd = KD[:, h * T:(h + 1) * T]
                    for t in range(NT):
                        lo, hi = t * P, min((t + 1) * P, T)
                        last = Cs3[:, h, hi - 1:hi].to_broadcast([P, hi - lo])
                        ins = pool.tensor_tensor(kd[:, lo:hi], Cs3[:, h, lo:hi], last, ALU.subtract)
                ins.then_inc(gp, 1)
                pool.wait_ge(ga, 4)
                pool.wait_ge(gv, 11)
                pool.tensor_tensor(QI, Q, QI, ALU.mult).then_inc(gp, 1)
                pool.tensor_tensor(KD, K, KD, ALU.mult).then_inc(gp, 1)
                n = 5
                for li, half in enumerate(LEVELS):
                    if half:
                        pool.wait_ge(lv_e, li)
                        pool.wait_ge(gl_mm, n)
                        if half == 64:
                            k3, s3 = (t.rearrange("p (h t) -> p h t", h=GH)[:, :, 0:TP] for t in (kt, K))
                            pool.tensor_tensor(k3, s3, d3[:, :, 0:TP], ALU.mult).then_inc(lv_k, 1)
                        else:
                            pool.tensor_tensor(kt, K, dt_, ALU.mult).then_inc(lv_k, 1)
                            n += 5
                pool.wait_ge(s_new, 4 * NT)
                pool.dma_start(gla_p[0, 0].rearrange("h k e -> k h e"), SP_[:, :, :]).then_inc(stored, 16)
                pool.dma_start(gla_s[0, 0].rearrange("h k e -> k h e"), SS[:, :, :]).then_inc(stored, 16)
                pool.wait_ge(gv, GV_MS + 6)
                pool.tensor_tensor(SQ[:, :, :], SQ[:, :, :], G[:, :, :], ALU.mult).then_inc(gp, 1)
                pool.wait_ge(gp, 4)
                for c in range(KC):
                    pool.wait_ge(gv, GV_MS + 6 + c + 1)
                    pool.tensor_tensor(O[:, c, :], O[:, c, :], SQ[:, c, :], ALU.mult).then_inc(g_ready, 1)

            for layer in range(4):
                if layer in (0, 3):
                    stick_breaking(layer, layer // 3)
                elif layer == 1:
                    convolution(layer)
                else:
                    linear_attention(layer)
                b = first_slab(layer) + IN_SLABS
                pool.wait_ge(chunk_done, 2 * b + 4)
                add_squares(2 * layer + 1)
                b = first_slab(layer) + LAYER_SLABS - OUT_SLABS
                pool.wait_ge(chunk_done, 2 * b + 4)
                add_squares(2 * layer + 2)
                if layer in (1, 2):
                    pool.wait_ge(chunk_done, 2 * first_slab(layer + 1) + 3)
                if layer == 1:
                    made(pool.memset(rankw[:, :, :, :].bitcast(F32), 0.0))
                    pool.wait_ge(rank_in, 16)
                    pool.tensor_copy(rankw[:, 0, :, 0:16], rank_raw[:]).then_inc(rank_hi, 1)
                    pool.wait_ge(rank_mm, 1)
                    pool.dma_start(SS, state_gla[0, 0].rearrange("h k e -> k h e")).then_inc(gs_in, 16)
                    pool.dma_start(wgk, gla_w_gk2[0]).then_inc(wgk_in, 16)
                    made(pool.memset(reset, 1.0))
                    pool.memset(reset[:, 0:T:P], 0.0).then_inc(reset_ready, 1)
                if layer == 2:
                    pool.dma_start(CK, cache_sb_k[1, 0].rearrange("(j p) h d -> p j (h d)", p=P)).then_inc(ck_in, 16)

            pool.wait_ge(ev_v, batches_before(TB_END, 0))
            pool.wait_ge(ev_a, batches_before(TB_END, 1))
            pool.dma_start(y_prompt[0].rearrange("(t p) f -> p t f", p=P), VT[:, 0:4, :]).then_inc(stored, 16)
            pool.dma_start(y_sample[0], VT[0:TS, 4, :]).then_inc(stored, 16)


STORES = 4 + 2 + 2
CONSTS = 6
VEC_DMAS = 7
GA_SQ = 7
GV_MS = 15

INPUTS = ["x_prompt", "x_sample", "cache_sb_k", "cache_sb_v", "state_conv", "state_gla", "norm_mix", "norm_mlp",
          "sb_w_qkv", "sb_w_o", "conv_w_in", "conv_w", "conv_w_out", "gla_w_in", "gla_w_gk2", "gla_b_gk", "gla_norm",
          "gla_w_o", "mlp_w_up", "mlp_w_down", "norm_final"]
OUTPUTS = [(1, 512, 1024), (1, 64, 1024), (2, 1, 512, 16, 64), (2, 1, 512, 16, 64), (2, 1, 64, 16, 64),
           (2, 1, 64, 16, 64), (1, 1, 2, 1024), (1, 1, 2, 1024), (1, 1, 4, 128, 256), (1, 1, 4, 128, 256)]


def kernel(**inputs):
    import numpy as np
    import concourse.bacc as bacc
    from concourse.bass_utils import run_bass_kernel_spmd

    nc = bacc.Bacc("TRN2", target_bir_lowering=False, num_devices=1)
    arrays, args = {}, []
    for name in INPUTS:
        a = np.ascontiguousarray(inputs[name])
        arrays[f"in_{name}"] = a
        args.append(nc.dram_tensor(f"in_{name}", a.shape, mybir.dt.from_np(a.dtype), kind="ExternalInput").ap())
    for i, shape in enumerate(OUTPUTS):
        args.append(nc.dram_tensor(f"out_{i}", shape, F32, kind="ExternalOutput").ap())
    trunk(nc, *args)
    r = run_bass_kernel_spmd(nc, [arrays], core_ids=[0])
    return tuple(r.results[0][f"out_{i}"] for i in range(len(OUTPUTS)))
```
